# Optimizing a Trainium2 kernel written in Bass

```python
import math
import jax, jax.numpy as jnp
from jax import lax
import numpy as np

D_MODEL = 1024
BATCH = 1
SEQ = 512
DEPTH = 2

GRID_W = 64
CTX_LEN = 256
EPS = 1e-6
DA_HEADS = 4
DA_QK = 64
DA_V = 2 * DA_QK
DA_WIDTH = DA_HEADS * DA_V
ROPE_BASE = 10000.0
Q_BLOCK = 128
ML_HEADS = 4
ML_DH = 128
ML_WIDTH = ML_HEADS * ML_DH
ML_CHUNK = 128
SHORT_CONV = 3
CV_WIDTH = 512
N_BRANCH = 3
D_IN = 3 * DA_WIDTH + 4 * ML_WIDTH + 4 * ML_HEADS + 3 * CV_WIDTH + N_BRANCH * D_MODEL
PEER_HEADS = 8
PEER_NKEYS = 128
PEER_N = PEER_NKEYS * PEER_NKEYS
PEER_DKEY = 256
PEER_TOPK = 16
PEER_BLOCK = 128

kernel_name = "hybrid_diffattn_mlstm_conv_peer_dit"

def rmsnorm(x, g):
    x32 = x.astype(jnp.float32)
    y = x32 * lax.rsqrt(jnp.mean(x32 * x32, axis=-1, keepdims=True) + EPS)
    return (y * g.astype(jnp.float32)).astype(x.dtype)

def modulate(h, shift, scale):
    return h * (1 + scale) + shift

def split_cols(z):
    sizes = [DA_WIDTH, DA_WIDTH, DA_WIDTH, 2 * ML_WIDTH, ML_WIDTH, ML_WIDTH, 4 * ML_HEADS,
             CV_WIDTH, CV_WIDTH, CV_WIDTH, N_BRANCH * D_MODEL]
    offs = np.cumsum(sizes)[:-1].tolist()
    return jnp.split(z, offs, axis=-1)

def conv3(x, w):
    ch = x.shape[-1]
    return lax.conv_general_dilated(x, w[:, None, :].astype(x.dtype), window_strides=(1,),
                                    padding=((SHORT_CONV // 2, SHORT_CONV // 2),),
                                    dimension_numbers=('NWC', 'WIO', 'NWC'),
                                    feature_group_count=ch)

def axial_rope(x, row, col):
    quarter = DA_QK // 4
    inv = ROPE_BASE ** (-jnp.arange(quarter, dtype=jnp.float32) / quarter)

    def rot(xp, pos):
        ang = pos.astype(jnp.float32)[:, None] * inv[None, :]
        cos = jnp.cos(ang)[None, :, None, None, :].astype(x.dtype)
        sin = jnp.sin(ang)[None, :, None, None, :].astype(x.dtype)
        x1, x2 = jnp.split(xp, 2, axis=-1)
        return jnp.concatenate([x1 * cos - x2 * sin, x1 * sin + x2 * cos], axis=-1)

    xr, xc = jnp.split(x, 2, axis=-1)
    return jnp.concatenate([rot(xr, row), rot(xc, col)], axis=-1)

def diff_attention(qc, kc, vc, ql, kl, vl, lam, lam_init, subln_g, need_ctx):
    B, S, _ = ql.shape
    rows = S // GRID_W
    row = jnp.repeat(jnp.arange(rows), GRID_W)
    col = jnp.tile(jnp.arange(GRID_W), rows)

    def heads_qk(a):
        return a.reshape(a.shape[0], a.shape[1], DA_HEADS, 2, DA_QK)

    def heads_v(a):
        return a.reshape(a.shape[0], a.shape[1], DA_HEADS, DA_V)

    ql = axial_rope(heads_qk(ql), row, col)
    kl = axial_rope(heads_qk(kl), row, col)
    qc, kc, vc = heads_qk(qc), heads_qk(kc), heads_v(vc)
    k_all = jnp.concatenate([kc, kl], axis=1)
    v_all = jnp.concatenate([vc, heads_v(vl)], axis=1)
    scale = DA_QK ** -0.5

    def attend(q, k, v):
        s = jnp.einsum('bqhmd,bkhmd->bhmqk', q, k).astype(jnp.float32) * scale
        a = jax.nn.softmax(s, axis=-1)
        w = (a[:, :, 0] - lam * a[:, :, 1]).astype(v.dtype)
        return jnp.einsum('bhqk,bkhe->bqhe', w, v)

    def finish(o):
        T = o.shape[1]
        o = rmsnorm(o, subln_g) * (1.0 - lam_init)
        return o.reshape(o.shape[0], T, DA_WIDTH)

    nb = S // Q_BLOCK
    qb = jnp.moveaxis(ql.reshape(B, nb, Q_BLOCK, DA_HEADS, 2, DA_QK), 1, 0)
    ol = lax.map(lambda q: attend(q, k_all, v_all), qb)
    ol = finish(jnp.moveaxis(ol, 0, 1).reshape(B, S, DA_HEADS, DA_V))
    oc = finish(attend(qc, kc, vc)) if need_ctx else None
    return oc, ol

def mlstm_chunk(carry, inp):
    C, n, m = carry
    q, k, v, ig, lf = inp
    L = q.shape[2]
    b = jnp.cumsum(lf, axis=-1)
    seen = jnp.tril(jnp.ones((L, L), dtype=bool))
    log_d = jnp.where(seen, b[..., :, None] - b[..., None, :] + ig[..., None, :], -jnp.inf)
    m_path = b + m[..., None]
    m_t = jnp.maximum(m_path, jnp.max(log_d, axis=-1))
    d = jnp.exp(log_d - m_t[..., None])
    carry_w = jnp.exp(m_path - m_t)
    w = jnp.einsum('bhtd,bhsd->bhts', q, k) * d
    num = jnp.einsum('bhts,bhse->bhte', w, v) + carry_w[..., None] * jnp.einsum('bhtd,bhde->bhte', q, C)
    den = jnp.sum(w, axis=-1) + carry_w * jnp.einsum('bhtd,bhd->bht', q, n)
    h = num / jnp.maximum(jnp.abs(den), jnp.exp(-m_t))[..., None]
    b_end = b[..., -1]
    log_w = b_end[..., None] - b + ig
    m_new = jnp.maximum(b_end + m, jnp.max(log_w, axis=-1))
    wk = jnp.exp(log_w - m_new[..., None])
    decay = jnp.exp(b_end + m - m_new)
    C_new = decay[..., None, None] * C + jnp.einsum('bhs,bhsd,bhse->bhde', wk, k, v)
    n_new = decay[..., None] * n + jnp.einsum('bhs,bhsd->bhd', wk, k)
    return (C_new, n_new, m_new), h

def mlstm_scan(q, k, v, ig, lf, state):
    B, H, T, d = q.shape
    nc = T // ML_CHUNK

    def to_chunks(a):
        return jnp.moveaxis(a.reshape(a.shape[:2] + (nc, ML_CHUNK) + a.shape[3:]), 2, 0)

    state, h = lax.scan(mlstm_chunk, state, (to_chunks(q), to_chunks(k), to_chunks(v), to_chunks(ig), to_chunks(lf)))
    h = jnp.moveaxis(h, 0, 2).reshape(B, H, T, d)
    return h, state

def mlstm_mixer(qk_c, v_c, o_c, g_c, qk_l, v_l, o_l, g_l, conv_w, gate_b, norm_g, need_ctx):
    def prep(qk, v, gates):
        qk = jax.nn.silu(conv3(qk, conv_w))
        q, k = jnp.split(qk, 2, axis=-1)
        B, T, _ = q.shape

        def hd(a):
            return a.reshape(B, T, ML_HEADS, ML_DH).transpose(0, 2, 1, 3).astype(jnp.float32)

        g = (gates.reshape(B, T, 4, ML_HEADS) + gate_b).astype(jnp.float32).transpose(2, 0, 3, 1)
        fwd = (g[0], jax.nn.log_sigmoid(g[1]))
        bwd = (g[2], jax.nn.log_sigmoid(g[3]))
        return hd(q), hd(k) * (ML_DH ** -0.5), hd(v), fwd, bwd

    qc, kc, vc, gfc, gbc = prep(qk_c, v_c, g_c)
    ql, kl, vl, gfl, gbl = prep(qk_l, v_l, g_l)
    B = ql.shape[0]
    zero = (jnp.zeros((B, ML_HEADS, ML_DH, ML_DH), jnp.float32),
            jnp.zeros((B, ML_HEADS, ML_DH), jnp.float32),
            jnp.zeros((B, ML_HEADS), jnp.float32))

    def flip(a):
        return jnp.flip(a, axis=2)

    hc_f, st_f = mlstm_scan(qc, kc, vc, gfc[0], gfc[1], zero)
    hl_f, _ = mlstm_scan(ql, kl, vl, gfl[0], gfl[1], st_f)
    hc_b, st_b = mlstm_scan(flip(qc), flip(kc), flip(vc), flip(gbc[0]), flip(gbc[1]), zero)
    hl_b, _ = mlstm_scan(flip(ql), flip(kl), flip(vl), flip(gbl[0]), flip(gbl[1]), st_b)

    def out(h, o):
        Bh, H, T, d = h.shape
        h = rmsnorm(h.transpose(0, 2, 1, 3), norm_g.reshape(H, d)).reshape(Bh, T, H * d)
        return (h * jax.nn.sigmoid(o.astype(jnp.float32))).astype(o.dtype)

    yl = out(hl_f + flip(hl_b), o_l)
    yc = out(hc_f + flip(hc_b), o_c) if need_ctx else None
    return yc, yl

def short_conv(bg, cg, xv, w):
    return bg * conv3(cg * xv, w)

def merge(y_da, y_ml, y_cv, gate, w_da, w_ml, w_cv, w_o):
    g = jax.nn.sigmoid(gate.astype(jnp.float32)).astype(y_da.dtype)
    g_da, g_ml, g_cv = jnp.split(g, N_BRANCH, axis=-1)
    m = g_da * (y_da @ w_da) + g_ml * (y_ml @ w_ml) + g_cv * (y_cv @ w_cv)
    return m @ w_o

def token_mixers(hc, hl, w_in, ml_gate_b, ml_conv_w, ml_norm_g, cv_conv_w, da_lam, da_subln_g,
                 w_da, w_ml, w_cv, w_o, lam_init, need_ctx):
    zc = split_cols(hc @ w_in)
    zl = split_cols(hl @ w_in)
    lv = da_lam.astype(jnp.float32)
    lam = jnp.exp(jnp.sum(lv[0] * lv[1])) - jnp.exp(jnp.sum(lv[2] * lv[3])) + lam_init
    da_c, da_l = diff_attention(zc[0], zc[1], zc[2], zl[0], zl[1], zl[2], lam, lam_init, da_subln_g, need_ctx)
    ml_c, ml_l = mlstm_mixer(zc[3], zc[4], zc[5], zc[6], zl[3], zl[4], zl[5], zl[6],
                             ml_conv_w, ml_gate_b, ml_norm_g, need_ctx)
    cv_l = short_conv(zl[7], zl[8], zl[9], cv_conv_w)
    out_l = merge(da_l, ml_l, cv_l, zl[10], w_da, w_ml, w_cv, w_o)
    out_c = None
    if need_ctx:
        cv_c = short_conv(zc[7], zc[8], zc[9], cv_conv_w)
        out_c = merge(da_c, ml_c, cv_c, zc[10], w_da, w_ml, w_cv, w_o)
    return out_c, out_l

def peer(h, wq, keys, u_tab, v_tab):
    B, T, D = h.shape
    N = B * T
    K = PEER_TOPK
    x = h.reshape(N, D)
    q = (x @ wq).reshape(N, PEER_HEADS, 2, PEER_DKEY // 2)
    s = jnp.einsum('nhpd,hpkd->nhpk', q, keys).astype(jnp.float32)
    top_s, top_i = lax.top_k(s, K)
    cand = top_s[:, :, 0, :, None] + top_s[:, :, 1, None, :]
    best_s, best = lax.top_k(cand.reshape(N, PEER_HEADS, K * K), K)
    i1 = jnp.take_along_axis(top_i[:, :, 0], best // K, axis=-1)
    i2 = jnp.take_along_axis(top_i[:, :, 1], best % K, axis=-1)
    expert = (i1 * PEER_NKEYS + i2).reshape(N, PEER_HEADS * K)
    gate = jax.nn.softmax(best_s, axis=-1).reshape(N, PEER_HEADS * K).astype(h.dtype)
    nb = N // PEER_BLOCK

    def block(args):
        xb, eb, gb = args
        a = jax.nn.gelu(jnp.einsum('tkd,td->tk', u_tab[eb], xb), approximate=False)
        return jnp.einsum('tk,tkd->td', gb * a, v_tab[eb])

    y = lax.map(block, (x.reshape(nb, PEER_BLOCK, D),
                        expert.reshape(nb, PEER_BLOCK, PEER_HEADS * K),
                        gate.reshape(nb, PEER_BLOCK, PEER_HEADS * K)))
    return y.reshape(B, T, D)

def setup_inputs(seed: int = 0) -> dict:
    key = jax.random.key(seed)
    ks = jax.random.split(key, 26)

    def nrm(k, shape, s):
        return jax.random.normal(k, shape, jnp.float32) * s

    f_bias = jnp.linspace(3.0, 6.0, ML_HEADS, dtype=jnp.float32)
    zb = jnp.zeros((ML_HEADS,), jnp.float32)
    gate_base = jnp.stack([zb, f_bias, zb, f_bias])
    return {
        "x": nrm(ks[0], (BATCH, SEQ, D_MODEL), 1.0),
        "c": nrm(ks[1], (BATCH, D_MODEL), 1.0),
        "ctx": nrm(ks[2], (BATCH, CTX_LEN, D_MODEL), 1.0),
        "c_ctx": nrm(ks[3], (D_MODEL,), 1.0),
        "w_ada": nrm(ks[4], (DEPTH, D_MODEL, 6 * D_MODEL), D_MODEL ** -0.5),
        "b_ada": nrm(ks[5], (DEPTH, 6 * D_MODEL), 0.02),
        "norm1_g": 1.0 + nrm(ks[6], (DEPTH, D_MODEL), 0.02),
        "norm2_g": 1.0 + nrm(ks[7], (DEPTH, D_MODEL), 0.02),
        "w_in": nrm(ks[8], (DEPTH, D_MODEL, D_IN), D_MODEL ** -0.5),
        "ml_gate_b": gate_base[None] + nrm(ks[9], (DEPTH, 4, ML_HEADS), 0.1),
        "ml_conv_w": nrm(ks[10], (DEPTH, SHORT_CONV, 2 * ML_WIDTH), SHORT_CONV ** -0.5),
        "ml_norm_g": 1.0 + nrm(ks[11], (DEPTH, ML_WIDTH), 0.02),
        "cv_conv_w": nrm(ks[12], (DEPTH, SHORT_CONV, CV_WIDTH), SHORT_CONV ** -0.5),
        "da_lam": nrm(ks[13], (DEPTH, 4, DA_QK), 0.1),
        "da_subln_g": 1.0 + nrm(ks[14], (DEPTH, DA_V), 0.02),
        "w_da": nrm(ks[15], (DEPTH, DA_WIDTH, D_MODEL), DA_WIDTH ** -0.5),
        "w_ml": nrm(ks[16], (DEPTH, ML_WIDTH, D_MODEL), ML_WIDTH ** -0.5),
        "w_cv": nrm(ks[17], (DEPTH, CV_WIDTH, D_MODEL), CV_WIDTH ** -0.5),
        "w_o": nrm(ks[18], (DEPTH, D_MODEL, D_MODEL), D_MODEL ** -0.5),
        "peer_wq": nrm(ks[19], (DEPTH, D_MODEL, PEER_HEADS * PEER_DKEY), D_MODEL ** -0.5),
        "peer_keys": nrm(ks[20], (DEPTH, PEER_HEADS, 2, PEER_NKEYS, PEER_DKEY // 2), (PEER_DKEY // 2) ** -0.5),
        "peer_u": nrm(ks[21], (DEPTH, PEER_N, D_MODEL), D_MODEL ** -0.5),
        "peer_v": nrm(ks[22], (DEPTH, PEER_N, D_MODEL), 0.5),
        "final_g": 1.0 + nrm(ks[23], (D_MODEL,), 0.02),
    }

def reference(x, c, ctx, c_ctx, w_ada, b_ada, norm1_g, norm2_g, w_in, ml_gate_b, ml_conv_w, ml_norm_g,
              cv_conv_w, da_lam, da_subln_g, w_da, w_ml, w_cv, w_o, peer_wq, peer_keys, peer_u, peer_v,
              final_g):
    xl, xc = x, ctx
    for l in range(DEPTH):
        need_ctx = l < DEPTH - 1
        lam_init = 0.8 - 0.6 * math.exp(-0.3 * l)
        sh1, sc1, g1, sh2, sc2, g2 = jnp.split(jax.nn.silu(c) @ w_ada[l] + b_ada[l], 6, axis=-1)
        csh1, csc1, cg1, csh2, csc2, cg2 = jnp.split(jax.nn.silu(c_ctx) @ w_ada[l] + b_ada[l], 6, axis=-1)
        hl = modulate(rmsnorm(xl, norm1_g[l]), sh1[:, None], sc1[:, None])
        hc = modulate(rmsnorm(xc, norm1_g[l]), csh1, csc1)
        out_c, out_l = token_mixers(hc, hl, w_in[l], ml_gate_b[l], ml_conv_w[l], ml_norm_g[l], cv_conv_w[l],
                                    da_lam[l], da_subln_g[l], w_da[l], w_ml[l], w_cv[l], w_o[l], lam_init, need_ctx)
        xl = xl + g1[:, None] * out_l
        hl = modulate(rmsnorm(xl, norm2_g[l]), sh2[:, None], sc2[:, None])
        xl = xl + g2[:, None] * peer(hl, peer_wq[l], peer_keys[l], peer_u[l], peer_v[l])
        if need_ctx:
            xc = xc + cg1 * out_c
            hc = modulate(rmsnorm(xc, norm2_g[l]), csh2, csc2)
            xc = xc + cg2 * peer(hc, peer_wq[l], peer_keys[l], peer_u[l], peer_v[l])
    return rmsnorm(xl, final_g)


_drawn_inputs = setup_inputs


def setup_inputs(seed=0):
    import zlib

    import numpy as np

    out = dict(_drawn_inputs(seed))
    spreads = {}
    factors = {'ml_norm_g': 3.622, 'da_subln_g': 2.967, 'final_g': 2.937}
    for name, (base, spread) in spreads.items():
        noise = np.random.default_rng([zlib.crc32(name.encode()), seed]).standard_normal(out[name].shape)
        drawn = base * np.exp(spread * noise) if base else spread * noise
        out[name] = __import__('jax').numpy.asarray(drawn.astype(out[name].dtype))
    for name, factor in factors.items():
        out[name] = (out[name] * factor).astype(out[name].dtype)
    return out
```

```python
import math
from contextlib import ExitStack

import numpy as np
import concourse.bass as bass
from concourse import mybir

D, SEQ, CTX, DEPTH, P = 1024, 512, 256, 2, 128
EPS = 1e-6
NT, CT = (SEQ + CTX) // P, CTX // P
TOK = NT * P
KD = D // P
GRID_W, ROPE_BASE = 64, 10000.0
H, DQ = 4, 64
W5 = 512
CH = W5 // P
COLS = dict(q=0, k=512, v=1024, mlqk=1536, mlv=2560, mlo=3072, gates=3584, bg=3600, cg=4112, xv=4624, gate=5136)
PH, NK, TOPK, PEER_N = 8, 128, 16, 16384
HP = 2 * PH
ADA_W = 384
BIG = 1e30

def build(nc, io):
    fp32, u32 = mybir.dt.float32, mybir.dt.uint32
    ALU, ACT, AX = mybir.AluOpType, mybir.ActivationFunctionType, mybir.AxisListType
    es = ExitStack()
    with es:
        sbuf = es.enter_context(nc.sbuf_tensor("arena", [P, 53200], fp32))
        psum = es.enter_context(nc.psum_tensor("psum", [P, 4096], fp32))
        ada_rows = nc.dram_tensor("ada_rows", [DEPTH * 2, 6 * D], fp32).ap()
        h2_rows = nc.dram_tensor("h2_rows", [TOK, D], fp32).ap()

        def sem(name):
            return es.enter_context(nc.semaphore(name))

        def view(base, shape, parts=P):
            n = int(np.prod(shape))
            ap = sbuf[0:parts, base:base + n]
            if len(shape) == 2:
                return ap.rearrange("p (a b) -> p a b", a=shape[0])
            if len(shape) == 3:
                return ap.rearrange("p (a b c) -> p a b c", a=shape[0], b=shape[1])
            return ap

        def bank(b, width=512, parts=P):
            return psum[0:parts, b * 512:b * 512 + width]

        at = [0]

        def keep(n):
            at[0] += n
            return at[0] - n

        X = view(keep(NT * D), [NT, D])
        IDENT = view(keep(P), [P])
        MASK = view(keep(2 * P), [2, P])
        ONES = view(keep(1), [1])
        SEL_AT = keep(8 * P)
        SEL = view(SEL_AT, [8, P], 36)
        COS = view(keep(4 * 32), [4, 32])
        SIN = view(keep(4 * 32), [4, 32])
        CCOL = view(keep(2 * KD), [2, KD])
        MLCW = view(keep(DEPTH * 24), [DEPTH, 8, 3])
        CVCW = view(keep(DEPTH * 12), [DEPTH, 4, 3])
        GATEB = view(keep(DEPTH), [DEPTH], 16)
        LAM = view(keep(DEPTH), [DEPTH])
        SMALL = keep(256)
        SS, MS, RS = view(SMALL, [24]), view(SMALL + 24, [24]), view(SMALL + 48, [24])
        MX, NM, SUM, RC, RL = (view(SMALL + 72 + 2 * i, [2]) for i in range(5))
        INV0 = view(SMALL + 84, [2])
        ZROW = view(keep(P), [P], 1)
        M0 = 8320
        assert at[0] <= M0, at[0]

        YD_AT, YM_AT, MLV_AT, MLO_AT, V_AT, KT_AT, QT_AT, HT_AT, MLT_AT, CVT_AT, W_AT, MISC = (
            M0 + x for x in (0, 3072, 6144, 9216, 12288, 15360, 18432, 21504, 27648, 33792, 36864, 43008))
        YD, YM, MLV, MLO, V = (view(a, [NT, W5]) for a in (YD_AT, YM_AT, MLV_AT, MLO_AT, V_AT))
        KT, QT, CVT = (view(a, [H, TOK]) for a in (KT_AT, QT_AT, CVT_AT))
        HT = view(HT_AT, [KD, TOK])
        MLT = view(MLT_AT, [8, TOK])
        G16 = view(MISC + 1024, [TOK], 16)

        phase_end = sem("phase_end")
        const_in, const_ready = sem("const_in"), sem("const_ready")
        w_in = [sem("w_in0"), sem("w_in1")]
        w_used = sem("w_used")
        stored = sem("stored")
        S = {}

        tok, chan, unit = 12 * NT, 21, NT * H
        first_layer = dict(
            mods1=80, mods2=80, normed1=NT, normed2=NT, n1_turned=NT, n2_turned=NT, n1_out=NT, n2_out=NT,
            ss1=1, ss2=1, ms1=1, ms2=1, root1=1, root2=1,
            tok_done=tok, tok_out=tok, chan_done=chan, chan_out=chan, conved=chan, roped=2,
            da_s=unit, da_max=unit, da_exp=unit, da_w=unit, da_turned=unit, da_wt=unit, da_o=unit, da_oout=unit,
            da_ms=1, da_root=1, da_normed=1, da_yturned=NT, da_yout=NT,
            nrow=32, rows_clear=1, gate_rows=64, ml_abs=1, ml_e=1, ml_e1=1, ml_ln=1, ml_args=1, ml_rows=1, ml_cols=1, ml_colout=1,
            ml_arg=2 * NT, ml_d=2 * NT, ml_wt=2 * NT, ml_a=2 * NT, ml_b=2 * NT, ml_kw=2 * NT, ml_state=2 * NT,
            ml_sig=1, ml_ms=1, ml_root=1, ml_normed=1, ml_yturned=NT, ml_yout=NT,
            g1=32, mg_done=12 * NT, mg_sig=12 * NT, mg_prod=12 * NT, mg_sum=1, mg_turned=NT, mg_out=NT, wo_done=4 * NT, wo_out=4 * NT,
            h2_out0=8 * NT, h2_out1=8 * NT, keys=16, rt_q=HP, rt_qout=HP, rt_s=HP, rt_sout=HP, rt_top=HP,
            added=NT + 1, x_taken=NT + 1, x_in=16 * NT, g2=32, routed=PH * (NT + 1), dots=4 * PH * NT, gelu=4 * PH * NT,
            diag=4 * PH * NT, soft_in=NT + 1, soft_out=NT + 1, summed=NT, lam_dot=1, lam_exp=1)

        def s(name):
            if name not in S:
                S[name] = sem(name)
            return S[name]

        def nth(l, name, n):
            return n + first_layer[name] if l else n

        def tiles(l):
            return list(range(NT)) if l < DEPTH - 1 else list(range(CT, NT))

        def chan_from(l, name, c):
            queries = name == "mlqk" and c < 2
            return CTX if l == DEPTH - 1 and (name == "cv" or queries) else 0

        def lam_init(l):
            return 0.8 - 0.6 * math.exp(-0.3 * l)

        def cols(w, c0, n, kd=KD):
            return w[:, c0:c0 + n].rearrange("(k p) n -> p k n", p=P), n, kd

        w_loads = []
        for l in range(DEPTH):
            for c in range(6 * D // ADA_W):
                w_loads.append((("ada", l, c), [(0, *cols(io["w_ada"][l], c * ADA_W, ADA_W))], 0))
        PHASES = ["norm1", "proj", "da", "ml", "merge", "norm2", "route", "peer"]

        def phase_no(l, name):
            return 1 + l * len(PHASES) + PHASES.index(name)

        def proj_steps(l):
            out = []
            for name in ("q", "k"):
                out += [("tok", name, c) for c in range(2)]
            out += [("turn", "q", 0)] + [("tok", "v", c) for c in range(2)] + [("turn", "k", 0)]
            out += [("tok", name, c) for name in ("mlv", "mlo") for c in range(2)]
            out += [("chan", "mlqk", c) for c in range(4)] + [("chan", "gates", 0)] + [("chan", "cv", c) for c in range(4)]
            return out

        for l in range(DEPTH):
            win = io["w_in"][l]
            for kind, name, c in proj_steps(l):
                if kind == "turn":
                    continue
                if name == "gates":
                    parts = [(0, *cols(win, COLS["gates"], 16))]
                elif name == "cv":
                    parts = [(KD * P * i, *cols(win, COLS[b] + c * P, P)) for i, b in enumerate(("bg", "cg", "xv"))]
                else:
                    parts = [(0, *cols(win, COLS[name] + c * 256, 256))]
                w_loads.append((("proj", l, kind, name, c), parts, phase_no(l, "norm1") if l else 0))
            for c in range(4):
                for b, wb in enumerate(("w_da", "w_ml", "w_cv")):
                    w_loads.append((("merge", l, c, b), [(0, *cols(win, COLS["gate"] + b * D + c * 256, 256)),
                                                         (2048, *cols(io[wb][l], c * 256, 256, CH))], phase_no(l, "merge")))
            for c in range(4):
                w_loads.append((("wo", l, c), [(0, *cols(io["w_o"][l], c * 256, 256))], phase_no(l, "merge")))
            for c in range(8):
                w_loads.append((("wq", l, c), [(0, *cols(io["peer_wq"][l], c * 256, 256))], phase_no(l, "merge")))
        w_at, count = {}, [0, 0]
        for n, (key, parts, _) in enumerate(w_loads):
            count[n % 2] += 16 * len(parts)
            w_at[key] = (n, count[n % 2])

        def weights(pe, key):
            n, landed = w_at[key]
            pe.wait_ge(w_in[n % 2], landed)
            return W_AT + (n % 2) * 3072

        def end_phase(eng):
            eng.drain().then_inc(phase_end, 1)

        def start_phase(eng, no):
            if no:
                eng.wait_ge(phase_end, 4 * no)

        ROW2 = view(HT_AT, [6 * D], 2)
        BROW = view(QT_AT, [ADA_W * 2], 2)
        CRAW = view(MISC, [2, KD])
        LROW = view(MISC + 32, [DEPTH, 4 * DQ])

        def ada_jobs():
            return [(l, c) for l in range(DEPTH) for c in range(6 * D // ADA_W)]

        MODS = view(KT_AT, [2, 2, D])
        GROW = view(KT_AT + 4 * D, [D])
        HST = view(YD_AT, [2, D])

        def norm_tiles(l, which):
            return list(range(NT)) if which == 1 else tiles(l)

        E = view(YM_AT, [2, TOK])
        WM = view(YM_AT + 3 * TOK, [TOK])
        WT = view(MISC, [TOK])
        NROW = view(W_AT, [W5])
        SQ = view(YM_AT, [NT, W5])

        def da_units(l):
            return [(h, t, CT if t < CT else NT) for t in tiles(l) for h in range(H)]

        ROWS = [view(V_AT + TOK * i, [TOK], 36) for i in range(6)]
        RST = view(V_AT + TOK * 6, [TOK], 36)
        MPREV, GEND, DEC = (view(V_AT + TOK * 7 + 8 * i, [NT], 36) for i in range(3))
        t_at = W_AT + 512
        ARG, WT4, KW4, T24, CST, ND4 = (view(t_at + 512 * i, [H, P]) for i in range(6))
        t_at += 512 * 6
        COL = view(t_at, [NT, 4, 36])
        DECB = view(t_at + 864, [8, NT])
        NST = view(t_at + 864 + 48, [H])
        ND = view(t_at + 864 + 56, [3, H])

        def ml_units(l):
            out = []
            for d, order in enumerate(([0, 1, 2, 3, 4, 5], [1, 0, 5, 4, 3, 2])):
                for i, j in enumerate(order):
                    out.append((d, j, i == 0, i == NT - 1, j in tiles(l)))
            return out

        MACC = view(V_AT, [NT, D])
        SIG = view(MISC, [4, 256])
        TMP = view(YM_AT, [4, 256])
        G1 = view(MLV_AT, [2, D])

        def merge_jobs(l):
            return [(c, b, t) for c in range(4) for b in range(3) for t in tiles(l)]

        TS = view(M0, [(NT + 1) * HP * TOPK])
        TI = view(M0 + 1792, [(NT + 1) * HP * TOPK])
        IDX = sbuf[:, M0 + 3584:M0 + 3584 + 896].bitcast(u32)
        GATE = view(M0 + 4480, [896])
        XT, XLD = view(M0 + 5376, [D]), view(M0 + 6400, [D])
        DIAG = view(M0 + 7424, [TOPK, P])
        G2 = view(M0 + 9472, [D])
        CAND, CANDW, OH, OH2 = (view(M0 + 10496 + 256 * i, [TOPK, TOPK]) for i in range(4))
        r_at = M0 + 11520
        TSH, TIH = view(r_at, [2, TOPK]), view(r_at + 32, [2, TOPK])
        BS, BF, BB = view(r_at + 64, [TOPK]), view(r_at + 80, [2, TOPK]), sbuf[:, r_at + 112:r_at + 160].bitcast(u32)
        IE = view(r_at + 160, [2, TOPK])
        IOTA = view(r_at + 192, [TOPK])
        ACTS, GELU, GH = view(r_at + 208, [TOPK]), view(r_at + 224, [TOPK]), view(r_at + 240, [TOPK])
        SMX, SSM = view(r_at + 256, [PH]), view(r_at + 264, [PH])
        IDH = sbuf[:, r_at + 272:r_at + 304].bitcast(u32).rearrange("p (a b) -> p a b", a=2)
        RING_AT = 53200 - 16 * 2048
        assert r_at + 304 <= RING_AT
        RING = view(RING_AT, [TOPK, 2 * D])
        KEYS = view(V_AT, [HP, P])
        KEYT = view(V_AT + 2048, [2, P])
        QST, SCO, SCW = (view(V_AT + 2304 + 1536 * i, [2, TOK]) for i in range(3))
        IXU = sbuf[:, V_AT + 6912:V_AT + 6912 + 192].bitcast(u32).rearrange("p (a b c) -> p a b c", a=2, b=NT)
        assert V_AT + 6912 + 192 <= HT_AT
        slots_free = sem("slots_free")
        gathered = [sem(f"gathered{k}") for k in range(TOPK)]

        def head_base(l):
            return sum(PH * len(tiles(i)) for i in range(l))

        streams = lambda l: ([(0, 0, CT)] if l < DEPTH - 1 else []) + [(1, CT, NT)]

        block = es.enter_context(nc.Block())

        @block.sync
        def _(sp):
            n_const = [0]

            def const(dst, src):
                sp.dma_start(dst, src).then_inc(const_in, 16)
                n_const[0] += 16

            const(CRAW[:, 0, :], io["c_cols"])
            const(CRAW[:, 1, :], io["cctx_cols"])
            for t in range(NT):
                src = io["ctx"][0] if t < CT else io["x"][0]
                t0 = t if t < CT else t - CT
                const(X[:, t, :], src[t0 * P:(t0 + 1) * P, :])
            const(COS.rearrange("p a b -> p (a b)"), io["rope_cos"])
            const(SIN.rearrange("p a b -> p (a b)"), io["rope_sin"])
            const(MLCW.rearrange("p a b c -> p (a b c)"), io["mlcw"])
            const(CVCW.rearrange("p a b c -> p (a b c)"), io["cvcw"])
            const(GATEB, io["gate_b"])
            const(LROW.rearrange("p a b -> p (a b)"), io["da_lam"].rearrange("(o l) a d -> o (l a d)", o=1).to_broadcast([P, DEPTH * 4 * DQ]))
            assert n_const[0] == CONST_DMAS * 16

            state = {"w": 0}

            def load_weights(upto):
                while state["w"] < len(w_loads) and w_loads[state["w"]][0][:2] != upto:
                    n = state["w"]
                    key, parts, phase = w_loads[n]
                    start_phase(sp, phase)
                    if n >= 2:
                        sp.wait_ge(w_used, n - 1)
                    for off, src, width, blocks in parts:
                        dst = view(W_AT + (n % 2) * 3072 + off, [blocks, width])
                        sp.dma_start(dst, src).then_inc(w_in[n % 2], 16)
                    if key[0] == "ada":
                        i = n
                        if i >= 2:
                            sp.wait_ge(s("ada_out"), i - 1)
                        sp.dma_start(BROW[:, (i % 2) * ADA_W:(i % 2 + 1) * ADA_W],
                                     io["b_ada"][key[1]:key[1] + 1, key[2] * ADA_W:(key[2] + 1) * ADA_W].to_broadcast([2, ADA_W])
                                     ).then_inc(s(f"brow{i % 2}"), 16)
                        if key[2] == 6 * D // ADA_W - 1:
                            sp.wait_ge(s("ada_out"), i + 1)
                            sp.dma_start(ada_rows[2 * key[1]:2 * key[1] + 2, :], ROW2).then_inc(stored, 16)
                    state["w"] += 1

            def norm_loads(l, which):
                no = phase_no(l, f"norm{which}")
                start_phase(sp, no)
                base = 0 if which == 1 else 3
                if which == 1 and l == 0:
                    sp.wait_ge(stored, 16 * DEPTH)
                for st in range(2):
                    row = ada_rows[2 * l + 1 - st:2 * l + 2 - st, :]
                    sp.dma_start(MODS[:, st, 0, :], row[:, (base + 1) * D:(base + 2) * D].to_broadcast([P, D])).then_inc(s(f"mods{which}"), 16)
                    sp.dma_start(MODS[:, st, 1, :], row[:, base * D:(base + 1) * D].to_broadcast([P, D])).then_inc(s(f"mods{which}"), 16)
                sp.dma_start(GROW, io[f"norm{which}_g"][l:l + 1, :].to_broadcast([P, D])).then_inc(s(f"mods{which}"), 16)

            load_weights(("proj", 0))
            for l in range(DEPTH):
                norm_loads(l, 1)
                load_weights(("merge", l))
                start_phase(sp, phase_no(l, "da"))
                sp.dma_start(NROW[:, 0:P], io["da_subln_g"][l:l + 1, :].to_broadcast([P, P])).then_inc(s("nrow"), 16)
                start_phase(sp, phase_no(l, "ml"))
                sp.dma_start(NROW, io["ml_norm_g"][l:l + 1, :].to_broadcast([P, W5])).then_inc(s("nrow"), 16)
                sp.wait_ge(s("rows_clear"), nth(l, "rows_clear", 1))
                for g, (row, p0) in enumerate(((0, 0), (1, 0), (0, 32), (1, 32))):
                    sp.dma_start(ROWS[row][p0:p0 + 4, :], G16[4 * g:4 * g + 4, :]).then_inc(s("gate_rows"), 16)
                start_phase(sp, phase_no(l, "merge"))
                for st in range(2):
                    sp.dma_start(G1[:, st, :], ada_rows[2 * l + 1 - st:2 * l + 2 - st, 2 * D:3 * D].to_broadcast([P, D])).then_inc(s("g1"), 16)
                load_weights(("wq", l))
                norm_loads(l, 2)
                for i, t in enumerate(norm_tiles(l, 2)):
                    sp.wait_ge(s("normed2"), nth(l, "normed2", i + 1))
                    sp.dma_start(h2_rows[t * P:(t + 1) * P, :], HST[:, i % 2, :]).then_inc(s(f"h2_out{i % 2}"), 16)
                for i in range(2):
                    sp.wait_ge(s(f"h2_out{i}"), nth(l, f"h2_out{i}", 8 * len(tiles(l))))
                start_phase(sp, phase_no(l, "route"))
                sp.dma_start(KEYS, io["peer_keys"][l].rearrange("h p k d -> k (h p) d")).then_inc(s("keys"), 16)
                load_weights(("proj", l + 1))
                start_phase(sp, phase_no(l, "peer"))
                i = 0
                for st, t0, t1 in streams(l):
                    if i:
                        sp.wait_ge(s("added"), nth(l, "added", i + 1))
                    sp.dma_start(G2, ada_rows[2 * l + 1 - st:2 * l + 2 - st, 5 * D:6 * D].to_broadcast([P, D])).then_inc(s("g2"), 16)
                    for t in range(t0, t1):
                        sp.wait_ge(s("x_taken"), nth(l, "x_taken", i + 1))
                        sp.dma_start(XLD, h2_rows[t * P:(t + 1) * P, :]).then_inc(s("x_in"), 16)
                        i += 1
            start_phase(sp, phase_no(DEPTH, "norm1"))
            sp.dma_start(GROW, io["final_g"].rearrange("(o d) -> o d", o=1).to_broadcast([P, D])).then_inc(s("final_g"), 16)
            for i, t in enumerate(range(CT, NT)):
                sp.wait_ge(s("final"), i + 1)
                sp.dma_start(io["out"][0, i * P:(i + 1) * P, :], X[:, t, :]).then_inc(stored, 16)
            sp.wait_ge(stored, 16 * (DEPTH + NT - CT))

        @block.gpsimd
        def _(pool):
            pool.memset(IDENT, 0.0)
            pool.memset(MASK.rearrange("p a b -> p (a b)"), 0.0)
            pool.memset(SEL.rearrange("p a b -> p (a b)"), 0.0)
            pool.memset(ONES, 1.0)
            pool.memset(ZROW, 0.0)
            pool.drain()
            pool.affine_select(out=IDENT, in_=IDENT, compare_op=ALU.not_equal, fill=1.0, base=0, pattern=[[-1, P]], channel_multiplier=1)
            pool.affine_select(out=MASK[:, 0, :], in_=MASK[:, 0, :], compare_op=ALU.is_ge, fill=BIG, base=0, pattern=[[1, P]], channel_multiplier=-1)
            pool.affine_select(out=MASK[:, 1, :], in_=MASK[:, 1, :], compare_op=ALU.is_ge, fill=BIG, base=0, pattern=[[-1, P]], channel_multiplier=1)
            for half in range(2):
                part = SEL[:, 4 * half:4 * half + 4, :]
                pool.affine_select(out=part, in_=part, compare_op=ALU.not_equal, fill=1.0, base=-32 * half, pattern=[[-1, 4], [0, P]], channel_multiplier=1)
            pool.drain().then_inc(const_ready, 1)
            end_phase(pool)
            for l in range(DEPTH):
                for name in PHASES:
                    start_phase(pool, phase_no(l, name))
                    if name == "peer":
                        b = head_base(l)
                        with pool.Fori(0, PH * len(tiles(l)), 2) as i:
                            for par in range(2):
                                pool.wait_ge(s("routed"), nth(l, "routed", i + par + 1))
                                pool.tensor_copy(IDH[:, par, :], IDX[:, bass.ds((i + par) * TOPK, TOPK)])
                                pool.drain()
                                for k in range(TOPK):
                                    if k % 4 == 0:
                                        pool.wait_ge(slots_free, (i + (b + par)) * 4 + (k // 4 + 1))
                                        pool.sem_inc(s("slots_given"), 1)
                                    pool.indirect_dma_start(RING[:, k, :], None, io["uv"],
                                                            bass.IndirectOffsetOnAxis(IDH[:, par, k:k + 1], 0)).then_inc(gathered[k], 16)
                    end_phase(pool)

        @block.scalar
        def _(act):
            A = nc.scalar
            act.wait_ge(const_in, 16 * CONST_DMAS)
            A.activation(CCOL, CRAW, ACT.Silu).then_inc(s("csilu"), 1)
            for l in range(DEPTH):
                act.wait_ge(s("lam_dot"), nth(l, "lam_dot", 1))
                A.activation(SUM, MX, ACT.Exp).then_inc(s("lam_exp"), 1)
            end_phase(act)

            def norm(l, which, ts):
                for t in ts:
                    A.activation(view(YM_AT, [2, D])[:, t % 2, :], X[:, t, :], ACT.Square, accum_out=SS[:, t:t + 1])
                    act.drain()
                act.drain().then_inc(s(f"ss{which}"), 1)
                act.wait_ge(s(f"ms{which}"), nth(l, f"ms{which}", 1))
                A.activation(RS[:, 0:NT], MS[:, 0:NT], ACT.Sqrt).then_inc(s(f"root{which}"), 1)

            def turned_out(l, name, dst, ts):
                for i, t in enumerate(ts):
                    act.wait_ge(s(name + "_turned"), nth(l, name + "_turned", i + 1))
                    A.activation(dst[:, :, t * P:(t + 1) * P], psum[:, (i % 2) * 1024:(i % 2 + 1) * 1024].rearrange("p (a b) -> p a b", a=KD), ACT.Copy).then_inc(s(name + "_out"), 1)

            for l in range(DEPTH):
                start_phase(act, phase_no(l, "norm1"))
                norm(l, 1, norm_tiles(l, 1))
                turned_out(l, "n1", HT, norm_tiles(l, 1))
                end_phase(act)

                start_phase(act, phase_no(l, "proj"))
                dest = dict(q=YD, k=MLO, v=V, mlv=MLV, mlo=MLO)
                n = c_n = 0
                for kind, name, c in proj_steps(l):
                    if kind == "tok":
                        for t in (tiles(l) if name in ("q", "mlo") else range(NT)):
                            act.wait_ge(s("tok_done"), nth(l, "tok_done", n + 1))
                            A.activation(dest[name][:, t, c * 256:(c + 1) * 256], bank(n % 4, 256), ACT.Copy).then_inc(s("tok_out"), 1)
                            n += 1
                    elif kind == "turn":
                        for t in (tiles(l) if name == "q" else range(NT)):
                            act.wait_ge(s("tok_done"), nth(l, "tok_done", n + 1))
                            A.activation((QT if name == "q" else KT)[:, :, t * P:(t + 1) * P], bank(n % 4).rearrange("p (a b) -> p a b", a=H), ACT.Copy).then_inc(s("tok_out"), 1)
                            n += 1
                    elif name == "gates":
                        act.wait_ge(s("chan_done"), nth(l, "chan_done", c_n + 1))
                        A.activation(G16, psum[0:16, 2048 + (c_n % 2) * 1024:2048 + (c_n % 2) * 1024 + TOK], ACT.Identity, bias=GATEB[:, l:l + 1]).then_inc(s("chan_out"), 1)
                        c_n += 1
                    else:
                        for i in range(2 if name == "mlqk" else 3):
                            act.wait_ge(s("chan_done"), nth(l, "chan_done", c_n + 1))
                            if c_n >= 4:
                                act.wait_ge(s("conved"), nth(l, "conved", c_n - 3))
                            c0 = chan_from(l, name, c)
                            p0 = 2048 + (c_n % 2) * 1024
                            A.activation(view(YM_AT, [4, TOK])[:, c_n % 4, c0:TOK], psum[:, p0 + c0:p0 + TOK], ACT.Copy).then_inc(s("chan_out"), 1)
                            c_n += 1
                act.wait_ge(s("conved"), nth(l, "conved", 9))
                for m in range(8):
                    c0 = chan_from(l, "mlqk", m // 2)
                    A.activation(MLT[:, m, c0:], MLT[:, m, c0:], ACT.Silu)
                end_phase(act)

                start_phase(act, phase_no(l, "da"))
                units = da_units(l)

                def exps(u):
                    nk = units[u][2] * P
                    act.wait_ge(s("da_max"), nth(l, "da_max", u + 1))
                    for m in range(2):
                        last = A.activation(E[:, m, 0:nk], psum[:, m * 1024:m * 1024 + nk], ACT.Exp, bias=NM[:, m:m + 1], scale=DQ ** -0.5, accum_out=SUM[:, m:m + 1])
                    last.then_inc(s("da_exp"), 1)

                exps(0)
                for u, (h, t, nk) in enumerate(units):
                    act.wait_ge(s("da_turned"), nth(l, "da_turned", u + 1))
                    if u:
                        act.wait_ge(s("da_o"), nth(l, "da_o", u))
                    A.activation(WT[:, 0:nk * P], psum[:, 2048:2048 + nk * P], ACT.Copy).then_inc(s("da_wt"), 1)
                    if u + 1 < len(units):
                        exps(u + 1)
                act.wait_ge(s("da_ms"), nth(l, "da_ms", 1))
                A.activation(RS, MS, ACT.Sqrt).then_inc(s("da_root"), 1)
                for i, t in enumerate(tiles(l)):
                    act.wait_ge(s("da_yturned"), nth(l, "da_yturned", i + 1))
                    A.activation(QT[:, :, t * P:(t + 1) * P], bank(i % 2).rearrange("p (a b) -> p a b", a=H), ACT.Copy).then_inc(s("da_yout"), 1)
                end_phase(act)

                start_phase(act, phase_no(l, "ml"))
                act.wait_ge(s("ml_abs"), nth(l, "ml_abs", 1))
                A.activation(ROWS[2], ROWS[2], ACT.Exp, scale=-1.0).then_inc(s("ml_e"), 1)
                act.wait_ge(s("ml_e1"), nth(l, "ml_e1", 1))
                A.activation(ROWS[2], ROWS[2], ACT.Ln).then_inc(s("ml_ln"), 1)
                act.wait_ge(s("ml_args"), nth(l, "ml_args", 1))
                A.activation(ROWS[2], ROWS[2], ACT.Exp)
                A.activation(ROWS[3], ROWS[5], ACT.Exp, scale=-1.0)
                A.activation(ROWS[4], ROWS[4], ACT.Exp)
                A.activation(DEC, DEC, ACT.Exp)
                act.drain().then_inc(s("ml_rows"), 1)
                act.wait_ge(s("ml_cols"), nth(l, "ml_cols", 1))
                for half in range(2):
                    A.activation(COL[:, 3 * half:3 * half + 3], bank(half, 432).rearrange("p (a b c) -> p a b c", a=3, b=4), ACT.Copy)
                A.activation(DECB, bank(2, 48).rearrange("p (a b) -> p a b", a=8), ACT.Copy)
                act.drain().then_inc(s("ml_colout"), 1)
                for i, (d, j, first, last, want) in enumerate(ml_units(l)):
                    if want:
                        act.wait_ge(s("ml_arg"), nth(l, "ml_arg", i + 1))
                        A.activation(ARG, ARG, ACT.Exp, scale=-1.0).then_inc(s("ml_d"), 1)
                    else:
                        act.wait_ge(s("ml_a"), nth(l, "ml_a", i + 1))
                        act.drain().then_inc(s("ml_d"), 1)
                    if i:
                        act.wait_ge(s("ml_b"), nth(l, "ml_b", i))
                    if not last:
                        for h in range(H):
                            r = COL[:, j, 3, 32 * d + h:32 * d + h + 1]
                            A.activation(KW4[:, h, :], bank(2)[:, h * P:(h + 1) * P], ACT.Copy, scale=r)
                    act.drain().then_inc(s("ml_kw"), 1)
                A.activation(MLO[:, tiles(l)[0]:, :], MLO[:, tiles(l)[0]:, :], ACT.Sigmoid).then_inc(s("ml_sig"), 1)
                act.wait_ge(s("ml_ms"), nth(l, "ml_ms", 1))
                A.activation(RS, MS, ACT.Sqrt).then_inc(s("ml_root"), 1)
                for i, t in enumerate(tiles(l)):
                    act.wait_ge(s("ml_yturned"), nth(l, "ml_yturned", i + 1))
                    A.activation(MLT[:, 0:H, t * P:(t + 1) * P], bank(i % 2).rearrange("p (a b) -> p a b", a=H), ACT.Copy).then_inc(s("ml_yout"), 1)
                end_phase(act)

                start_phase(act, phase_no(l, "merge"))
                for n, (c, b, t) in enumerate(merge_jobs(l)):
                    act.wait_ge(s("mg_done"), nth(l, "mg_done", n + 1))
                    if n >= 4:
                        act.wait_ge(s("mg_prod"), nth(l, "mg_prod", n - 3))
                    A.activation(SIG[:, n % 4, :], bank(n % 8, 256), ACT.Sigmoid).then_inc(s("mg_sig"), 1)
                turned_out(l, "mg", HT, tiles(l))
                end_phase(act)

                start_phase(act, phase_no(l, "norm2"))
                norm(l, 2, norm_tiles(l, 2))
                turned_out(l, "n2", HT, norm_tiles(l, 2))
                end_phase(act)

                start_phase(act, phase_no(l, "route"))
                t0 = tiles(l)[0] * P
                for hp in range(HP):
                    act.wait_ge(s("rt_q"), nth(l, "rt_q", hp + 1))
                    if hp >= 2:
                        act.wait_ge(s("rt_s"), nth(l, "rt_s", hp - 1))
                    A.activation(QST[:, hp % 2, t0:TOK], psum[:, 3072 * (hp % 2) + t0:3072 * (hp % 2) + TOK], ACT.Copy)
                    A.activation(KEYT[:, hp % 2, :], bank(2 + hp % 2, P), ACT.Copy)
                    act.drain().then_inc(s("rt_qout"), 1)
                    act.wait_ge(s("rt_s"), nth(l, "rt_s", hp + 1))
                    if hp >= 2:
                        act.wait_ge(s("rt_top"), nth(l, "rt_top", hp - 1))
                    A.activation(SCO[:, hp % 2, t0:TOK], psum[:, 2048 + t0:2048 + TOK], ACT.Copy).then_inc(s("rt_sout"), 1)
                end_phase(act)

                start_phase(act, phase_no(l, "peer"))

                def soft(base, n):
                    act.wait_ge(s("soft_in"), nth(l, "soft_in", n))
                    A.activation(GATE[:, bass.ds(base, P)], GATE[:, bass.ds(base, P)], ACT.Exp).then_inc(s("soft_out"), 1)

                soft(0, 1)
                with act.Fori(0, len(tiles(l))) as ti:
                    with act.Fori(0, PH) as h:
                        for g in range(4):
                            act.wait_ge(s("dots"), nth(l, "dots", (ti * PH + h) * 4 + (g + 1)))
                            A.activation(GELU[:, 4 * g:4 * g + 4], ACTS[:, 4 * g:4 * g + 4], ACT.Gelu).then_inc(s("gelu"), 1)
                    soft((ti + 1) * P, ti + 2)
                end_phase(act)
            start_phase(act, phase_no(DEPTH, "norm1"))
            norm(0, 3, range(CT, NT))

        @block.vector
        def _(dve):
            V_ = nc.vector
            TT, TSC, STT = V_.tensor_tensor, V_.tensor_scalar, V_.scalar_tensor_tensor

            def bc(ap, shape):
                return ap.to_broadcast(shape)

            dve.wait_ge(const_in, 16 * CONST_DMAS)
            for l in range(DEPTH):
                for i in range(2):
                    V_.tensor_tensor_reduce(out=view(MISC + 600, [DQ]), in0=LROW[:, l, 2 * i * DQ:(2 * i + 1) * DQ], in1=LROW[:, l, (2 * i + 1) * DQ:(2 * i + 2) * DQ],
                                            scale=1.0, scalar=0.0, op0=ALU.mult, op1=ALU.add, accum_out=MX[:, i:i + 1])
                    dve.drain()
                dve.drain().then_inc(s("lam_dot"), 1)
                dve.wait_ge(s("lam_exp"), nth(l, "lam_exp", 1))
                TT(RL[:, 0:1], SUM[:, 0:1], SUM[:, 1:2], ALU.subtract)
                dve.drain()
                TSC(LAM[:, l:l + 1], RL[:, 0:1], lam_init(l), -1.0, ALU.add, ALU.mult)
                dve.drain()
            for i, (l, c) in enumerate(ada_jobs()):
                dve.wait_ge(s("ada_mm"), i + 1)
                dve.wait_ge(s(f"brow{i % 2}"), 16 * (i // 2 + 1))
                if c == 0 and l:
                    dve.wait_ge(stored, 16 * l)
                TT(ROW2[:, c * ADA_W:(c + 1) * ADA_W], bank(i % 4, ADA_W, 2), BROW[:, (i % 2) * ADA_W:(i % 2 + 1) * ADA_W], ALU.add).then_inc(s("ada_out"), 1)
            end_phase(dve)

            def roots(l, which, n, width):
                TSC(MS[:, 0:n], SS[:, 0:n], 1.0 / width, EPS, ALU.mult, ALU.add).then_inc(s(which + "ms" if which in ("da_", "ml_") else "ms" + which), 1)
                dve.wait_ge(s(which + "root" if which in ("da_", "ml_") else "root" + which), nth(l, which + "root" if which in ("da_", "ml_") else "root" + which, 1))
                V_.reciprocal(RS[:, 0:n], RS[:, 0:n])
                dve.drain()

            def norm(l, which, ts):
                V_.memset(SS, 1.0) if which == 3 else None
                dve.wait_ge(s(f"mods{which}"), nth(l, f"mods{which}", 80))
                for st in range(2):
                    STT(MODS[:, st, 0, :], MODS[:, st, 0, :], 1.0, GROW, ALU.add, ALU.mult)
                dve.wait_ge(s(f"ss{which}"), nth(l, f"ss{which}", 1))
                roots(l, str(which), NT, D)
                for i, t in enumerate(ts):
                    st = 0 if t < CT else 1
                    if i >= 2:
                        dve.wait_ge(s(f"n{which}_turned"), nth(l, f"n{which}_turned", i - 1))
                        if which == 2:
                            dve.wait_ge(s(f"h2_out{i % 2}"), nth(l, f"h2_out{i % 2}", 16 * (i // 2)))
                    STT(HST[:, i % 2, :], X[:, t, :], RS[:, t:t + 1], MODS[:, st, 0, :], ALU.mult, ALU.mult)
                    dve.drain()
                    TT(HST[:, i % 2, :], HST[:, i % 2, :], MODS[:, st, 1, :], ALU.add).then_inc(s(f"normed{which}"), 1)

            def conv3(dst, src, w, segs, c0):
                TSC(dst[:, c0:TOK], src[:, c0:TOK], w[:, 1:2], None, ALU.mult)
                dve.drain()
                for a, b in segs:
                    STT(dst[:, a + 1:b], src[:, a:b - 1], w[:, 0:1], dst[:, a + 1:b], ALU.mult, ALU.add)
                dve.drain()
                for a, b in segs:
                    STT(dst[:, a:b - 1], src[:, a + 1:b], w[:, 2:3], dst[:, a:b - 1], ALU.mult, ALU.add)
                dve.drain()

            def head_norm(l, which, t0, gain, gains):
                nh = (NT - t0) * H
                y = YD[:, t0:NT, :].rearrange("p t (h e) -> p (t h) e", h=H)
                sq = SQ[:, t0:NT, :].rearrange("p t (h e) -> p (t h) e", h=H)
                TT(sq, y, y, ALU.mult)
                V_.memset(SS, 1.0)
                dve.drain()
                V_.reduce_sum(SS[:, 0:nh], sq, AX.X)
                dve.drain()
                roots(l, which, 24, P)
                TT(sq, y, bc(RS[:, 0:nh].unsqueeze(2), [P, nh, P]), ALU.mult)
                dve.drain()
                if gain.shape[1] == P:
                    STT(y, sq, gains, bc(gain.unsqueeze(1), [P, nh, P]), ALU.mult, ALU.mult)
                else:
                    TT(YD[:, t0:NT, :], SQ[:, t0:NT, :], bc(gain.unsqueeze(1), [P, NT - t0, W5]), ALU.mult)
                dve.drain()

            def top16(vals, idx, sco, work):
                for v, i_, sc, w in zip(vals, idx, sco, work):
                    V_.max(v[:, 0:8], sc)
                dve.drain()
                for v, i_, sc, w in zip(vals, idx, sco, work):
                    V_.max_index(i_[:, 0:8], v[:, 0:8], sc)
                    V_.match_replace(w, v[:, 0:8], sc, -3e38)
                dve.drain()
                for v, i_, sc, w in zip(vals, idx, sco, work):
                    V_.max(v[:, 8:16], w)
                dve.drain()
                for v, i_, sc, w in zip(vals, idx, sco, work):
                    V_.max_index(i_[:, 8:16], v[:, 8:16], w)
                dve.drain()

            def route(l, head):
                V_.tensor_copy(TSH, TS[:, bass.ds(head * 32, 32)].rearrange("p (a b) -> p a b", a=2))
                V_.tensor_copy(TIH, TI[:, bass.ds(head * 32, 32)].rearrange("p (a b) -> p a b", a=2))
                dve.drain()
                TT(CAND, bc(TSH[:, 0, :].unsqueeze(2), [P, TOPK, TOPK]), bc(TSH[:, 1, :].unsqueeze(1), [P, TOPK, TOPK]), ALU.add)
                dve.drain()
                flat = lambda a: a.rearrange("p a b -> p (a b)")
                top16([BS], [BB[:, 0:16]], [flat(CAND)], [flat(CANDW)])
                TSC(BB[:, 16:32], BB[:, 0:16], 4, None, ALU.logical_shift_right)
                TSC(BB[:, 32:48], BB[:, 0:16], 15, None, ALU.bitwise_and)
                dve.drain()
                V_.tensor_copy(BF, BB[:, 16:48].rearrange("p (a b) -> p a b", a=2))
                dve.drain()
                oh = (OH, OH2)
                for i in range(2):
                    TT(oh[i], bc(BF[:, i, :].unsqueeze(2), [P, TOPK, TOPK]), bc(IOTA.unsqueeze(1), [P, TOPK, TOPK]), ALU.is_equal)
                dve.drain()
                for i in range(2):
                    TT(oh[i], oh[i], bc(TIH[:, i, :].unsqueeze(1), [P, TOPK, TOPK]), ALU.mult)
                dve.drain()
                for i in range(2):
                    V_.reduce_sum(IE[:, i, :], oh[i], AX.X)
                V_.tensor_copy(GATE[:, bass.ds(head * TOPK, TOPK)], BS)
                dve.drain()
                TSC(IE[:, 0, :], IE[:, 0, :], float(NK), float(l * PEER_N), ALU.mult, ALU.add)
                dve.drain()
                TT(IDX[:, bass.ds(head * TOPK, TOPK)], IE[:, 0, :], IE[:, 1, :], ALU.add).then_inc(s("routed"), 1)

            for l in range(DEPTH):
                t_lo = tiles(l)[0]
                start_phase(dve, phase_no(l, "norm1"))
                norm(l, 1, norm_tiles(l, 1))
                end_phase(dve)

                start_phase(dve, phase_no(l, "proj"))
                nq, nc_ = 2 * len(tiles(l)), 0
                for step, (buf, upto) in enumerate(((YD, nq), (MLO, nq + 2 * NT))):
                    dve.wait_ge(s("tok_out"), nth(l, "tok_out", upto))
                    for t in range(CT, NT):
                        x = buf[:, t, :].rearrange("p (g r two c) -> p g r two c", g=2 * H, r=2, two=2)
                        x1, x2 = x[:, :, :, 0, :], x[:, :, :, 1, :]
                        cos, sin = (bc(a[:, t - CT, :].rearrange("p (r c) -> p r c", r=2).unsqueeze(1), [P, 2 * H, 2, 16]) for a in (COS, SIN))
                        p = [view(MISC + 256 * i, [2 * H, 2, 16]) for i in range(4)]
                        for o, a, b in ((p[0], x1, cos), (p[1], x2, sin), (p[2], x1, sin), (p[3], x2, cos)):
                            TT(o, a, b, ALU.mult)
                        dve.drain()
                        TT(x1, p[0], p[1], ALU.subtract)
                        TT(x2, p[2], p[3], ALU.add)
                        dve.drain()
                    dve.drain().then_inc(s("roped"), 1)
                stage = view(YM_AT, [4, TOK])
                segs = [(0, CTX), (CTX, TOK)]
                for m in range(8):
                    dve.wait_ge(s("chan_out"), nth(l, "chan_out", m + 1))
                    c0 = chan_from(l, "mlqk", m // 2)
                    conv3(MLT[:, m, :], stage[:, m % 4, :], MLCW[:, l, m, :], segs if not c0 else segs[1:], c0)
                    dve.drain().then_inc(s("conved"), 1)
                dve.wait_ge(s("chan_out"), nth(l, "chan_out", 9))
                dve.drain().then_inc(s("conved"), 1)
                c0 = chan_from(l, "cv", 0)
                for m in range(CH):
                    j = 9 + 3 * m
                    dve.wait_ge(s("chan_out"), nth(l, "chan_out", j + 3))
                    bg, cg, xv = (stage[:, (j + i) % 4, :] for i in range(3))
                    TT(cg[:, c0:], cg[:, c0:], xv[:, c0:], ALU.mult)
                    dve.drain()
                    conv3(CVT[:, m, :], cg, CVCW[:, l, m, :], segs if not c0 else segs[1:], c0)
                    TT(CVT[:, m, c0:], CVT[:, m, c0:], bg[:, c0:], ALU.mult)
                    dve.drain().then_inc(s("conved"), 3)
                end_phase(dve)

                start_phase(dve, phase_no(l, "da"))
                units = da_units(l)

                def maxes(u):
                    nk = units[u][2] * P
                    dve.wait_ge(s("da_s"), nth(l, "da_s", u + 1))
                    V_.reduce_max(MX, psum[:, 0:2048].rearrange("p (m n) -> p m n", m=2)[:, :, 0:nk], AX.X)
                    dve.drain()
                    TSC(NM, MX, -(DQ ** -0.5), None, ALU.mult).then_inc(s("da_max"), 1)

                def outputs(u):
                    h, t, _ = units[u]
                    dve.wait_ge(s("da_o"), nth(l, "da_o", u + 1))
                    TSC(YD[:, t, h * P:(h + 1) * P], bank(6 + u % 2, P), INV0[:, u % 2:u % 2 + 1], None, ALU.mult).then_inc(s("da_oout"), 1)

                maxes(0)
                for u, (h, t, nk) in enumerate(units):
                    n = nk * P
                    dve.wait_ge(s("da_exp"), nth(l, "da_exp", u + 1))
                    V_.reciprocal(RC[:, 0:1], SUM[:, 1:2])
                    V_.reciprocal(INV0[:, u % 2:u % 2 + 1], SUM[:, 0:1])
                    dve.drain()
                    TSC(RL[:, 0:1], RC[:, 0:1], SUM[:, 0:1], LAM[:, l:l + 1], ALU.mult, ALU.mult)
                    dve.drain()
                    if u:
                        dve.wait_ge(s("da_turned"), nth(l, "da_turned", u))
                    STT(WM[:, 0:n], E[:, 1, 0:n], RL[:, 0:1], E[:, 0, 0:n], ALU.mult, ALU.add).then_inc(s("da_w"), 1)
                    if u + 1 < len(units):
                        dve.wait_ge(s("da_w"), nth(l, "da_w", u + 1))
                        maxes(u + 1)
                    if u:
                        outputs(u - 1)
                        dve.drain()
                outputs(len(units) - 1)
                dve.drain()
                dve.wait_ge(s("nrow"), nth(l, "nrow", 16))
                head_norm(l, "da_", t_lo, NROW[:, 0:P], 1.0 - lam_init(l))
                dve.drain().then_inc(s("da_normed"), 1)
                end_phase(dve)

                start_phase(dve, phase_no(l, "ml"))
                V_.memset(sbuf[0:36, V_AT:V_AT + 8 * TOK], 0.0)
                dve.drain()
                V_.memset(RST, 1.0)
                dve.drain()
                V_.memset(RST.rearrange("p (j t) -> p j t", t=P)[:, :, 0:1], 0.0)
                dve.drain().then_inc(s("rows_clear"), 1)
                TSC(MLT[:, 4:8, :], MLT[:, 4:8, :], P ** -0.5, None, ALU.mult)
                dve.wait_ge(s("gate_rows"), nth(l, "gate_rows", 64))
                ig, f, tmp, lf, b_, m_ = ROWS
                STT(tmp, f, -1.0, f, ALU.mult, ALU.max).then_inc(s("ml_abs"), 1)
                dve.wait_ge(s("ml_e"), nth(l, "ml_e", 1))
                TSC(tmp, tmp, 1.0, None, ALU.add).then_inc(s("ml_e1"), 1)
                dve.wait_ge(s("ml_ln"), nth(l, "ml_ln", 1))
                STT(lf, f, 0.0, tmp, ALU.min, ALU.subtract)
                dve.drain()
                scan = V_.tensor_tensor_scan
                scan(b_[0:4, :], RST[0:4, :], lf[0:4, :], 0.0, ALU.mult, ALU.add)
                scan(b_[32:36, ::-1], RST[32:36, :], lf[32:36, ::-1], 0.0, ALU.mult, ALU.add)
                scan(m_[0:4, :], lf[0:4, :], ig[0:4, :], 0.0, ALU.add, ALU.max)
                rev = lambda a, lo, hi: a[32:36, lo:hi][:, ::-1]
                scan(rev(m_, 0, CTX), rev(lf, 0, CTX), rev(ig, 0, CTX), 0.0, ALU.add, ALU.max)
                dve.drain()
                scan(rev(m_, CTX, TOK), rev(lf, CTX, TOK), rev(ig, CTX, TOK), m_[32:36, 0:1], ALU.add, ALU.max)
                dve.drain()
                TT(f, m_, b_, ALU.subtract)
                TT(ig, ig, b_, ALU.subtract)
                dve.drain()
                V_.tensor_copy(MPREV[0:4, 1:6], m_[0:4, P - 1:5 * P:P])
                V_.tensor_copy(MPREV[32:36, 2:5], m_[32:36, 3 * P:6 * P:P])
                V_.tensor_copy(MPREV[32:36, 5:6], m_[32:36, 0:1])
                V_.tensor_copy(MPREV[32:36, 0:1], m_[32:36, P:P + 1])
                V_.tensor_copy(GEND[0:4, :], f[0:4, P - 1:TOK:P])
                V_.tensor_copy(GEND[32:36, :], f[32:36, 0:TOK:P])
                dve.drain()
                r3 = lambda a: a.rearrange("p (j t) -> p j t", t=P)
                TT(r3(tmp), bc(MPREV.unsqueeze(2), [36, NT, P]), r3(f), ALU.subtract)
                TT(r3(b_), r3(ig), bc(GEND.unsqueeze(2), [36, NT, P]), ALU.subtract)
                TT(DEC, MPREV, GEND, ALU.subtract)
                dve.drain().then_inc(s("ml_args"), 1)
                dve.wait_ge(s("ml_colout"), nth(l, "ml_colout", 1))
                def arguments(i):
                    d, j, first, last, want = ml_units(l)[i]
                    if want:
                        dve.wait_ge(s("ml_a"), nth(l, "ml_a", i + 1))
                        for h in range(H):
                            STT(ARG[:, h, :], bank(0)[:, h * P:(h + 1) * P], COL[:, j, 0, 32 * d + h:32 * d + h + 1], MASK[:, d, :], ALU.subtract, ALU.max)
                    dve.drain().then_inc(s("ml_arg"), 1)

                def within(i):
                    if ml_units(l)[i][4]:
                        dve.wait_ge(s("ml_d"), nth(l, "ml_d", i + 1))
                        TT(WT4, bank(1).rearrange("p (h t) -> p h t", h=H), ARG, ALU.mult).then_inc(s("ml_wt"), 1)
                    else:
                        dve.drain().then_inc(s("ml_wt"), 1)

                arguments(0)
                within(0)
                for i, (d, j, first, last, want) in enumerate(ml_units(l)):
                    c = lambda k: COL[:, j, k, 32 * d:32 * d + H]
                    if i + 1 < 2 * NT:
                        arguments(i + 1)
                    dve.wait_ge(s("ml_b"), nth(l, "ml_b", i + 1))
                    if i + 1 < 2 * NT:
                        within(i + 1)
                    b3 = lambda k: bank(k).rearrange("p (h e) -> p h e", h=H)
                    aux = bank(6, 12).rearrange("p (k h) -> p k h", k=3)
                    dec = DECB[:, 4 * d:4 * d + 4, j]
                    if want and not first:
                        TT(T24, b3(4), bc(c(1).unsqueeze(2), [P, H, P]), ALU.mult)
                        TT(ND[:, 0, :], aux[:, 1, :], c(1), ALU.mult)
                    if not first and not last:
                        TT(CST, CST, bc(dec.unsqueeze(2), [P, H, P]), ALU.mult)
                        TT(NST, NST, dec, ALU.mult)
                    dve.drain()
                    if want and not first:
                        TT(T24, T24, b3(3), ALU.add)
                        TT(ND[:, 1, :], ND[:, 0, :], aux[:, 0, :], ALU.add)
                    elif want:
                        V_.tensor_copy(T24, b3(3))
                        V_.tensor_copy(ND[:, 1, :], aux[:, 0, :])
                    if first:
                        V_.tensor_copy(CST, b3(5))
                        V_.tensor_copy(NST, aux[:, 2, :])
                    elif not last:
                        TT(CST, CST, b3(5), ALU.add)
                        TT(NST, NST, aux[:, 2, :], ALU.add)
                    dve.drain().then_inc(s("ml_state"), 1)
                    if want:
                        STT(ND[:, 0, :], ND[:, 1, :], -1.0, ND[:, 1, :], ALU.mult, ALU.max)
                        dve.drain()
                        TT(ND[:, 0, :], ND[:, 0, :], c(2), ALU.max)
                        dve.drain()
                        V_.reciprocal(ND[:, 2, :], ND[:, 0, :])
                        dve.drain()
                        y = YD[:, j, :].rearrange("p (h e) -> p h e", h=H)
                        r = bc(ND[:, 2, :].unsqueeze(2), [P, H, P])
                        if d == 0:
                            TT(y, T24, r, ALU.mult)
                        else:
                            TT(ND4, T24, r, ALU.mult)
                            dve.drain()
                            TT(y, y, ND4, ALU.add)
                dve.drain()
                dve.wait_ge(s("nrow"), nth(l, "nrow", 32))
                head_norm(l, "ml_", t_lo, NROW, None)
                dve.wait_ge(s("ml_sig"), nth(l, "ml_sig", 1))
                TT(YD[:, t_lo:, :], YD[:, t_lo:, :], MLO[:, t_lo:, :], ALU.mult).then_inc(s("ml_normed"), 1)
                end_phase(dve)

                start_phase(dve, phase_no(l, "merge"))
                for n, (c, b, t) in enumerate(merge_jobs(l)):
                    dve.wait_ge(s("mg_sig"), nth(l, "mg_sig", n + 1))
                    m = MACC[:, t, c * 256:(c + 1) * 256]
                    prod = m if b == 0 else TMP[:, n % 4, :]
                    TT(prod, SIG[:, n % 4, :], bank(n % 8)[:, 256:512], ALU.mult).then_inc(s("mg_prod"), 1)
                    dve.drain()
                    if b:
                        TT(m, m, prod, ALU.add)
                        dve.drain()
                dve.drain().then_inc(s("mg_sum"), 1)
                dve.wait_ge(s("g1"), nth(l, "g1", 32))
                for n, (c, t) in enumerate([(c, t) for c in range(4) for t in tiles(l)]):
                    dve.wait_ge(s("wo_done"), nth(l, "wo_done", n + 1))
                    x = X[:, t, c * 256:(c + 1) * 256]
                    TT(TMP[:, n % 4, :], bank(4 + n % 4, 256), G1[:, 0 if t < CT else 1, c * 256:(c + 1) * 256], ALU.mult).then_inc(s("wo_out"), 1)
                    dve.drain()
                    TT(x, x, TMP[:, n % 4, :], ALU.add)
                end_phase(dve)

                start_phase(dve, phase_no(l, "norm2"))
                norm(l, 2, norm_tiles(l, 2))
                end_phase(dve)

                start_phase(dve, phase_no(l, "route"))
                for i in range(2):
                    dve.wait_ge(s(f"h2_out{i}"), nth(l, f"h2_out{i}", 8 * len(tiles(l))))
                V_.memset(TS, 0.0)
                V_.memset(TI, 0.0)
                for k in range(TOPK):
                    V_.memset(IOTA[:, k:k + 1], float(k))
                dve.drain()
                ts4, ti4 = (a.rearrange("p (t g k) -> p t g k", g=HP, k=TOPK) for a in (TS, TI))
                for hp in range(HP):
                    dve.wait_ge(s("rt_sout"), nth(l, "rt_sout", hp + 1))
                    ts_ = tiles(l)
                    top16([ts4[:, i, hp, :] for i in range(len(ts_))], [IXU[:, hp % 2, i, :] for i in range(len(ts_))],
                          [SCO[:, hp % 2, t * P:(t + 1) * P] for t in ts_], [SCW[:, hp % 2, t * P:(t + 1) * P] for t in ts_])
                    V_.tensor_copy(ti4[:, 0:len(ts_), hp, :], IXU[:, hp % 2, 0:len(ts_), :])
                    dve.drain().then_inc(s("rt_top"), 1)
                    if hp % 2:
                        route(l, hp // 2)
                        dve.drain()
                end_phase(dve)

                start_phase(dve, phase_no(l, "peer"))
                dve.drain().then_inc(s("x_taken"), 1)
                dve.drain().then_inc(s("added"), 1)

                def softmax(tile, n):
                    g = GATE[:, bass.ds(tile * P, P)].rearrange("p (h k) -> p h k", h=PH)
                    V_.tensor_copy(SMX.unsqueeze(2), g[:, :, 0:1])
                    dve.drain()
                    TT(g, g, bc(SMX.unsqueeze(2), [P, PH, TOPK]), ALU.subtract)
                    dve.drain().then_inc(s("soft_in"), 1)
                    dve.wait_ge(s("soft_out"), nth(l, "soft_out", n))
                    dve.sem_inc(s("wait_over"), 1)
                    V_.reduce_sum(SSM, g, AX.X)
                    dve.drain()
                    V_.reciprocal(SMX, SSM)
                    dve.drain()
                    TT(g, g, bc(SMX.unsqueeze(2), [P, PH, TOPK]), ALU.mult)
                    dve.drain()

                softmax(0, 1)
                first_tile = 0
                for si, (st, t0, t1) in enumerate(streams(l)):
                    dve.wait_ge(s("g2"), nth(l, "g2", 16 * (si + 1)))
                    with dve.Fori(0, t1 - t0) as tj:
                        dve.wait_ge(s("x_in"), nth(l, "x_in", (tj + (first_tile + 1)) * 16))
                        V_.tensor_copy(XT, XLD)
                        dve.drain().then_inc(s("x_taken"), 1)
                        with dve.Fori(0, PH) as h:
                            lin = (tj + first_tile) * PH + h
                            V_.tensor_copy(GH, GATE[:, bass.ds(lin * TOPK, TOPK)])
                            for g in range(4):
                                for k in range(4 * g, 4 * g + 4):
                                    dve.wait_ge(gathered[k], (lin + (head_base(l) + 1)) * 16)
                                    last = V_.tensor_tensor_reduce(out=psum[:, 1024 + (k % 2) * 1024:2048 + (k % 2) * 1024], in0=RING[:, k, 0:D], in1=XT, scale=1.0, scalar=0.0,
                                                            op0=ALU.mult, op1=ALU.add, accum_out=ACTS[:, k:k + 1])
                                    dve.drain()
                                dve.drain().then_inc(s("dots"), 1)
                                if g == 1:
                                    route(l, lin + PH)
                                dve.wait_ge(s("gelu"), nth(l, "gelu", lin * 4 + (g + 1)))
                                for k in range(4 * g, 4 * g + 4):
                                    TSC(DIAG[:, k, :], IDENT, GELU[:, k:k + 1], GH[:, k:k + 1], ALU.mult, ALU.mult)
                                dve.drain().then_inc(s("diag"), 1)
                        softmax(tj + (first_tile + 1), tj + (first_tile + 2))
                        dve.wait_ge(s("summed"), nth(l, "summed", tj + (first_tile + 1)))
                        TT(XT, psum[:, 0:D], G2, ALU.mult)
                        dve.drain()
                        x = X.rearrange("p t d -> p (t d)")[:, bass.ds((tj + t0) * D, D)]
                        TT(x, x, XT, ALU.add)
                        dve.drain().then_inc(s("added"), 1)
                    first_tile += t1 - t0
                end_phase(dve)

            start_phase(dve, phase_no(DEPTH, "norm1"))
            dve.wait_ge(s("final_g"), 16)
            dve.wait_ge(s("ss3"), 1)
            V_.memset(SS[:, 0:CT], 1.0)
            dve.drain()
            roots(0, "3", NT, D)
            for t in range(CT, NT):
                STT(X[:, t, :], X[:, t, :], RS[:, t:t + 1], GROW, ALU.mult, ALU.mult).then_inc(s("final"), 1)

        @block.tensor
        def _(pe):
            mm = nc.tensor.matmul

            def turn(out, in_, n=P):
                return mm(out, in_, IDENT[0:n, 0:n], start=True, stop=True, is_transpose=True)

            def used(ins):
                ins.then_inc(w_used, 1)

            pe.wait_ge(const_ready, 1)
            pe.wait_ge(s("csilu"), 1)
            for i, (l, c) in enumerate(ada_jobs()):
                w = view(weights(pe, ("ada", l, c)), [KD, ADA_W])
                if i >= 4:
                    pe.wait_ge(s("ada_out"), i - 3)
                for k in range(KD):
                    last = mm(bank(i % 4, ADA_W, 2), CCOL[:, :, k], w[:, k, :], start=(k == 0), stop=(k == KD - 1))
                last.then_inc(s("ada_mm"), 1)
                pe.wait_ge(s("ada_mm"), i + 1)
                pe.sem_inc(w_used, 1)
            pe.drain().then_inc(slots_free, 4)
            end_phase(pe)

            def norm(l, which, ts):
                for i, t in enumerate(ts):
                    pe.wait_ge(s(f"normed{which}"), nth(l, f"normed{which}", i + 1))
                    if i >= 2:
                        pe.wait_ge(s(f"n{which}_out"), nth(l, f"n{which}_out", i - 1))
                    for k in range(KD):
                        last = turn(psum[:, (i % 2) * 1024 + k * P:(i % 2) * 1024 + (k + 1) * P], HST[:, i % 2, k * P:(k + 1) * P])
                    last.then_inc(s(f"n{which}_turned"), 1)

            def heads_turned(l, which):
                pe.wait_ge(s(which + "_normed"), nth(l, which + "_normed", 1))
                for i, t in enumerate(tiles(l)):
                    if i >= 2:
                        pe.wait_ge(s(which + "_yout"), nth(l, which + "_yout", i - 1))
                    for h in range(H):
                        last = turn(bank(i % 2)[:, h * P:(h + 1) * P], YD[:, t, h * P:(h + 1) * P])
                    last.then_inc(s(which + "_yturned"), 1)

            for l in range(DEPTH):
                start_phase(pe, phase_no(l, "norm1"))
                norm(l, 1, norm_tiles(l, 1))
                end_phase(pe)

                start_phase(pe, phase_no(l, "proj"))
                n = c_n = turns = 0
                for kind, name, c in proj_steps(l):
                    if kind == "turn":
                        pe.wait_ge(s("roped"), nth(l, "roped", turns + 1))
                        turns += 1
                        src = YD if name == "q" else MLO
                        for t in (tiles(l) if name == "q" else range(NT)):
                            if n >= 4:
                                pe.wait_ge(s("tok_out"), nth(l, "tok_out", n - 3))
                            for h in range(H):
                                last = turn(bank(n % 4)[:, h * P:(h + 1) * P], src[:, t, h * P:(h + 1) * P])
                            last.then_inc(s("tok_done"), 1)
                            n += 1
                        continue
                    base = weights(pe, ("proj", l, kind, name, c))
                    if kind == "tok":
                        w = view(base, [KD, 256])
                        for t in (tiles(l) if name in ("q", "mlo") else range(NT)):
                            if n >= 4:
                                pe.wait_ge(s("tok_out"), nth(l, "tok_out", n - 3))
                            for k in range(KD):
                                last = mm(bank(n % 4, 256), HT[:, k, t * P:(t + 1) * P], w[:, k, :], start=(k == 0), stop=(k == KD - 1))
                            last.then_inc(s("tok_done"), 1)
                            n += 1
                        pe.wait_ge(s("tok_done"), nth(l, "tok_done", n))
                    else:
                        if name == "gates":
                            blocks, lo = [view(base, [KD, 16])], 0
                        elif name == "mlqk":
                            blocks, lo = [view(base, [KD, 256])[:, :, i * P:(i + 1) * P] for i in range(2)], chan_from(l, name, c)
                        else:
                            blocks, lo = [view(base + KD * P * i, [KD, P]) for i in range(3)], chan_from(l, name, c)
                        for w in blocks:
                            if c_n >= 2:
                                pe.wait_ge(s("chan_out"), nth(l, "chan_out", c_n - 1))
                            m = w.shape[2]
                            p0 = 2048 + (c_n % 2) * 1024
                            for a, b in ((lo, 512), (512, TOK)):
                                for k in range(KD):
                                    last = mm(psum[0:m, p0 + a:p0 + b], w[:, k, :], HT[:, k, a:b], start=(k == 0), stop=(k == KD - 1))
                            last.then_inc(s("chan_done"), 1)
                            c_n += 1
                        pe.wait_ge(s("chan_done"), nth(l, "chan_done", c_n))
                    pe.sem_inc(w_used, 1)
                end_phase(pe)

                start_phase(pe, phase_no(l, "da"))
                units = da_units(l)

                def scores(u):
                    h, t, nk = units[u]
                    if u:
                        pe.wait_ge(s("da_exp"), nth(l, "da_exp", u))
                    for m in range(2):
                        rows = slice(DQ * m, DQ * m + DQ)
                        for a, b in ((0, min(nk * P, 512)), (512, nk * P)):
                            if b > a:
                                last = mm(psum[:, m * 1024 + a:m * 1024 + b], QT[rows, h, t * P:(t + 1) * P], KT[rows, h, a:b], start=True, stop=True)
                    last.then_inc(s("da_s"), 1)

                scores(0)
                for u, (h, t, nk) in enumerate(units):
                    if u + 1 < len(units):
                        scores(u + 1)
                    pe.wait_ge(s("da_w"), nth(l, "da_w", u + 1))
                    if u:
                        pe.wait_ge(s("da_wt"), nth(l, "da_wt", u))
                    for kt in range(nk):
                        last = turn(psum[:, 2048 + kt * P:2048 + (kt + 1) * P], WM[:, kt * P:(kt + 1) * P])
                    last.then_inc(s("da_turned"), 1)
                    pe.wait_ge(s("da_wt"), nth(l, "da_wt", u + 1))
                    if u >= 2:
                        pe.wait_ge(s("da_oout"), nth(l, "da_oout", u - 1))
                    for kt in range(nk):
                        last = mm(bank(6 + u % 2, P), WT[:, kt * P:(kt + 1) * P], V[:, kt, h * P:(h + 1) * P], start=(kt == 0), stop=(kt == nk - 1))
                    last.then_inc(s("da_o"), 1)
                heads_turned(l, "da")
                end_phase(pe)

                start_phase(pe, phase_no(l, "ml"))
                pe.wait_ge(s("ml_rows"), nth(l, "ml_rows", 1))
                arrays = (ROWS[0], ROWS[2], ROWS[3], ROWS[4])
                for j in range(NT):
                    for a, row in enumerate(arrays):
                        c0 = ((j % 3) * 4 + a) * 36
                        turn(bank(j // 3)[:, c0:c0 + 36], row[:, j * P:(j + 1) * P], 36)
                for r in range(8):
                    last = mm(bank(2)[:, r * NT:(r + 1) * NT], SEL[:, r, :], DEC, start=True, stop=True)
                last.then_inc(s("ml_cols"), 1)
                pe.wait_ge(s("ml_colout"), nth(l, "ml_colout", 1))
                def ahead(i):
                    d, j, first, last_, want = ml_units(l)[i]
                    tok = slice(j * P, (j + 1) * P)
                    if i:
                        pe.wait_ge(s("ml_wt"), nth(l, "ml_wt", i))
                        pe.wait_ge(s("ml_kw"), nth(l, "ml_kw", i))
                    for h in range(H):
                        o = slice(h * P, (h + 1) * P)
                        if want:
                            mm(bank(0)[:, o], SEL[:, 4 * d + h, :], ROWS[1][:, tok], start=True, stop=True)
                            mm(bank(1)[:, o], MLT[:, 4 + h, tok], MLT[:, h, tok], start=True, stop=True)
                        last = turn(bank(2)[:, o], MLT[:, 4 + h, tok])
                    last.then_inc(s("ml_a"), 1)

                ahead(0)
                for i, (d, j, first, last_, want) in enumerate(ml_units(l)):
                    tok = slice(j * P, (j + 1) * P)
                    if i + 1 < 2 * NT:
                        ahead(i + 1)
                    pe.wait_ge(s("ml_wt"), nth(l, "ml_wt", i + 1))
                    pe.wait_ge(s("ml_kw"), nth(l, "ml_kw", i + 1))
                    if i:
                        pe.wait_ge(s("ml_state"), nth(l, "ml_state", i))
                    aux = bank(6, 12).rearrange("p (k h) -> p k h", k=3)
                    last = None
                    for h in range(H):
                        o = slice(h * P, (h + 1) * P)
                        v = MLV[:, j, o]
                        if want:
                            mm(bank(3)[:, o], WT4[:, h, :], v, start=True, stop=True)
                            last = mm(aux[:, 0, h:h + 1], WT4[:, h, :], ONES, start=True, stop=True)
                            if not first:
                                mm(bank(4)[:, o], MLT[:, h, tok], CST[:, h, :], start=True, stop=True)
                                last = mm(aux[:, 1, h:h + 1], MLT[:, h, tok], NST[:, h:h + 1], start=True, stop=True)
                        if not last_:
                            mm(bank(5)[:, o], KW4[:, h, :], v, start=True, stop=True)
                            last = mm(aux[:, 2, h:h + 1], KW4[:, h, :], ONES, start=True, stop=True)
                    last.then_inc(s("ml_b"), 1)
                heads_turned(l, "ml")
                end_phase(pe)

                start_phase(pe, phase_no(l, "merge"))
                ys = (QT, MLT, CVT)
                n = 0
                for c in range(4):
                    for b in range(3):
                        base = weights(pe, ("merge", l, c, b))
                        wg, wb = view(base, [KD, 256]), view(base + 2048, [CH, 256])
                        for t in tiles(l):
                            tok = slice(t * P, (t + 1) * P)
                            if n >= 8:
                                pe.wait_ge(s("mg_prod"), nth(l, "mg_prod", n - 7))
                            for k in range(KD):
                                mm(bank(n % 8, 256), HT[:, k, tok], wg[:, k, :], start=(k == 0), stop=(k == KD - 1))
                            for k in range(CH):
                                last = mm(bank(n % 8)[:, 256:512], ys[b][:, k, tok], wb[:, k, :], start=(k == 0), stop=(k == CH - 1))
                            last.then_inc(s("mg_done"), 1)
                            n += 1
                        pe.wait_ge(s("mg_done"), nth(l, "mg_done", n))
                        pe.sem_inc(w_used, 1)
                pe.wait_ge(s("mg_sum"), nth(l, "mg_sum", 1))
                for i, t in enumerate(tiles(l)):
                    if i >= 2:
                        pe.wait_ge(s("mg_out"), nth(l, "mg_out", i - 1))
                    for k in range(KD):
                        last = turn(psum[:, (i % 2) * 1024 + k * P:(i % 2) * 1024 + (k + 1) * P], MACC[:, t, k * P:(k + 1) * P])
                    last.then_inc(s("mg_turned"), 1)
                pe.wait_ge(s("mg_out"), nth(l, "mg_out", len(tiles(l))))
                n = 0
                for c in range(4):
                    w = view(weights(pe, ("wo", l, c)), [KD, 256])
                    for t in tiles(l):
                        if n >= 4:
                            pe.wait_ge(s("wo_out"), nth(l, "wo_out", n - 3))
                        for k in range(KD):
                            last = mm(bank(4 + n % 4, 256), HT[:, k, t * P:(t + 1) * P], w[:, k, :], start=(k == 0), stop=(k == KD - 1))
                        last.then_inc(s("wo_done"), 1)
                        n += 1
                    pe.wait_ge(s("wo_done"), nth(l, "wo_done", n))
                    pe.sem_inc(w_used, 1)
                end_phase(pe)

                start_phase(pe, phase_no(l, "norm2"))
                norm(l, 2, norm_tiles(l, 2))
                end_phase(pe)

                start_phase(pe, phase_no(l, "route"))
                lo = tiles(l)[0] * P
                pe.wait_ge(s("keys"), nth(l, "keys", 16))
                wq_slot = {}

                def queries(hp):
                    if hp % 2 == 0:
                        wq_slot[0] = view(weights(pe, ("wq", l, hp // 2)), [KD, 256])
                    w, q0 = wq_slot[0], 3072 * (hp % 2)
                    if hp >= 2:
                        pe.wait_ge(s("rt_qout"), nth(l, "rt_qout", hp - 1))
                    for a, b in ((lo, 512), (512, TOK)):
                        for k in range(KD):
                            mm(psum[:, q0 + a:q0 + b], w[:, k, (hp % 2) * P:(hp % 2 + 1) * P], HT[:, k, a:b], start=(k == 0), stop=(k == KD - 1))
                    turn(bank(2 + hp % 2, P), KEYS[:, hp, :]).then_inc(s("rt_q"), 1)
                    if hp % 2:
                        pe.wait_ge(s("rt_q"), nth(l, "rt_q", hp + 1))
                        pe.sem_inc(w_used, 1)

                queries(0)
                for hp in range(HP):
                    if hp + 1 < HP:
                        queries(hp + 1)
                    pe.wait_ge(s("rt_qout"), nth(l, "rt_qout", hp + 1))
                    if hp:
                        pe.wait_ge(s("rt_sout"), nth(l, "rt_sout", hp))
                    for t in tiles(l):
                        last = mm(psum[:, 2048 + t * P:2048 + (t + 1) * P], QST[:, hp % 2, t * P:(t + 1) * P], KEYT[:, hp % 2, :], start=True, stop=True)
                    last.then_inc(s("rt_s"), 1)
                end_phase(pe)

                start_phase(pe, phase_no(l, "peer"))
                with pe.Fori(0, len(tiles(l))) as ti:
                    pe.wait_ge(s("added"), nth(l, "added", ti + 1))
                    for half in range(2):
                        mm(bank(half), ZROW, view(SEL_AT, [512], 1), start=True, stop=False, skip_group_check=True)
                    with pe.Fori(0, PH) as h:
                        for g in range(4):
                            pe.wait_ge(s("diag"), nth(l, "diag", (ti * PH + h) * 4 + (g + 1)))
                            for k in range(4 * g, 4 * g + 4):
                                for half in range(2):
                                    last = mm(bank(half), DIAG[:, k, :], RING[:, k, D + half * 512:D + (half + 1) * 512], start=False, stop=False, skip_group_check=True)
                            last.then_inc(slots_free, 1)
                    for half in range(2):
                        last = mm(bank(half), ZROW, view(SEL_AT, [512], 1), start=False, stop=True, skip_group_check=True)
                    last.then_inc(s("summed"), 1)
                end_phase(pe)

CONST_DMAS = 2 + NT + 6

def rope_tables():
    quarter = DQ // 4
    inv = (np.float32(ROPE_BASE) ** (-np.arange(quarter, dtype=np.float32) / np.float32(quarter))).astype(np.float32)
    n = np.arange(SEQ)
    ang = np.stack([(n // GRID_W).astype(np.float32)[:, None] * inv, (n % GRID_W).astype(np.float32)[:, None] * inv], 1)
    ang = ang.reshape(SEQ // P, P, 32).transpose(1, 0, 2).reshape(P, -1)
    return np.cos(ang).astype(np.float32), np.sin(ang).astype(np.float32)

def kernel(**inputs):
    import concourse.bacc as bacc
    from concourse.bass_utils import run_bass_kernel_spmd

    a = {k: np.ascontiguousarray(v) for k, v in inputs.items()}
    cos, sin = rope_tables()
    arrays = {k: a[k] for k in ("x", "ctx", "w_ada", "b_ada", "norm1_g", "norm2_g", "w_in", "ml_norm_g", "da_lam",
                                "da_subln_g", "w_da", "w_ml", "w_cv", "w_o", "peer_wq", "peer_keys", "final_g")}
    lay = np.ascontiguousarray
    arrays["c_cols"] = lay(a["c"].reshape(KD, P).T)
    arrays["cctx_cols"] = lay(a["c_ctx"].reshape(KD, P).T)
    arrays["mlcw"] = lay(a["ml_conv_w"].reshape(DEPTH, 3, 8, P).transpose(3, 0, 2, 1).reshape(P, -1))
    arrays["cvcw"] = lay(a["cv_conv_w"].reshape(DEPTH, 3, 4, P).transpose(3, 0, 2, 1).reshape(P, -1))
    arrays["gate_b"] = lay(a["ml_gate_b"].reshape(DEPTH, 16).T)
    arrays["uv"] = np.concatenate([a["peer_u"], a["peer_v"]], axis=-1).reshape(DEPTH * PEER_N, 2 * D)
    arrays["rope_cos"], arrays["rope_sin"] = cos, sin
    nc = bacc.Bacc("TRN2", target_bir_lowering=False, num_devices=1)
    io = {k: nc.dram_tensor("in_" + k, v.shape, mybir.dt.from_np(v.dtype), kind="ExternalInput").ap() for k, v in arrays.items()}
    io["out"] = nc.dram_tensor("out", (1, SEQ, D), mybir.dt.float32, kind="ExternalOutput").ap()
    build(nc, io)
    r = run_bass_kernel_spmd(nc, [{"in_" + k: v for k, v in arrays.items()}], core_ids=[0])
    return r.results[0]["out"]
```
